# Optimizing a Trainium2 kernel written in Bass

```python
import jax, jax.numpy as jnp
from jax import lax
import numpy as np
import math

D_MODEL = 1024
BATCH = 1
SEQ = 256
DEPTH = 2

N_A_LAYERS = DEPTH // 2
N_B_LAYERS = DEPTH - N_A_LAYERS
D_FF = 2816
CHUNK = 128
GMLP_HALF = 2 * D_MODEL
GMLP_GROUPS = 16
GMLP_GROUP_DIM = GMLP_HALF // GMLP_GROUPS
N_HEADS = 8
QK_NOPE = 128
QK_ROPE = 64
V_DIM = 128
KV_RANK = 256
Q_RANK = 512
Q_BLOCK = 128
ROPE_THETA = 10000.0
RMS_EPS = 1e-6
LN_EPS = 1e-5
NEG_INF = -1e30


def rms_norm(x, g):
    x32 = x.astype(jnp.float32)
    y = x32 * lax.rsqrt(jnp.mean(x32 * x32, axis=-1, keepdims=True) + RMS_EPS) * g.astype(jnp.float32)
    return y.astype(x.dtype)

def layer_norm(x, g, b):
    x32 = x.astype(jnp.float32)
    mu = jnp.mean(x32, axis=-1, keepdims=True)
    xc = x32 - mu
    y = xc * lax.rsqrt(jnp.mean(xc * xc, axis=-1, keepdims=True) + LN_EPS)
    return (y * g.astype(jnp.float32) + b.astype(jnp.float32)).astype(x.dtype)

def swiglu(n, w_gate, w_up, w_down):
    return (jax.nn.silu(n @ w_gate) * (n @ w_up)) @ w_down

def rope_tables(positions):
    inv_freq = ROPE_THETA ** (-jnp.arange(0, QK_ROPE, 2, dtype=jnp.float32) / QK_ROPE)
    ang = positions.astype(jnp.float32)[..., None] * inv_freq
    return jnp.cos(ang), jnp.sin(ang)

def apply_rope(x, cos, sin):
    cos = cos.astype(x.dtype)
    sin = sin.astype(x.dtype)
    x1, x2 = jnp.split(x, 2, axis=-1)
    return jnp.concatenate([x1 * cos - x2 * sin, x2 * cos + x1 * sin], axis=-1)

def gmlp_mixer(n, w_in, ln_g, ln_b, w_s, b_s, w_out):
    b, s, _ = n.shape
    z = jax.nn.gelu(n @ w_in)
    u, v = jnp.split(z, 2, axis=-1)
    v = layer_norm(v, ln_g, ln_b)
    v = v.reshape(b, s // CHUNK, CHUNK, GMLP_GROUPS, GMLP_GROUP_DIM)
    causal = jnp.tril(jnp.ones((CHUNK, CHUNK), dtype=w_s.dtype))
    w = w_s * causal
    sv = jnp.einsum('gtc,bncgd->bntgd', w, v) + jnp.transpose(b_s)[None, None, :, :, None]
    return (u * sv.reshape(b, s, GMLP_HALF)) @ w_out

def shared_kv(h, kv_norm_g, w_dkv, kv_a_norm_g, w_ukv, cos, sin):
    b, s, _ = h.shape
    n = rms_norm(h, kv_norm_g)
    ckv = n @ w_dkv
    c, k_rope = ckv[..., :KV_RANK], ckv[..., KV_RANK:]
    c = rms_norm(c, kv_a_norm_g)
    k_rope = apply_rope(k_rope, cos, sin)
    kv = (c @ w_ukv).reshape(b, s, N_HEADS, QK_NOPE + V_DIM)
    return kv[..., :QK_NOPE], k_rope, kv[..., QK_NOPE:]

def mla_mixer(n, k_nope, k_rope, v, w_dq, q_norm_g, w_uq, w_o, cos, sin):
    b, s, _ = n.shape
    q = (rms_norm(n @ w_dq, q_norm_g) @ w_uq).reshape(b, s, N_HEADS, QK_NOPE + QK_ROPE)
    q_nope = q[..., :QK_NOPE]
    q_rope = apply_rope(q[..., QK_NOPE:], cos[:, :, None, :], sin[:, :, None, :])
    scale = (QK_NOPE + QK_ROPE) ** -0.5
    outs = []
    for blk in range(s // Q_BLOCK):
        q0, q1 = blk * Q_BLOCK, (blk + 1) * Q_BLOCK
        sc = (jnp.einsum('bqhd,bkhd->bhqk', q_nope[:, q0:q1], k_nope[:, :q1])
              + jnp.einsum('bqhr,bkr->bhqk', q_rope[:, q0:q1], k_rope[:, :q1]))
        sc = sc.astype(jnp.float32) * scale
        q_idx = q0 + jnp.arange(Q_BLOCK)
        k_idx = jnp.arange(q1)
        sc = jnp.where(k_idx[None, :] <= q_idx[:, None], sc, NEG_INF)
        p = jax.nn.softmax(sc, axis=-1).astype(v.dtype)
        outs.append(jnp.einsum('bhqk,bkhd->bqhd', p, v[:, :q1]))
    o = jnp.concatenate(outs, axis=1).reshape(b, s, N_HEADS * V_DIM)
    return o @ w_o

def first_inputs(seed: int = 0) -> dict:
    key = jax.random.key(seed)
    ks = iter(jax.random.split(key, 40))

    def w(shape, fan_in):
        return jax.random.normal(next(ks), shape, jnp.float32) * (fan_in ** -0.5)

    def g(shape):
        return 1.0 + 0.02 * jax.random.normal(next(ks), shape, jnp.float32)

    x = jax.random.normal(next(ks), (BATCH, SEQ, D_MODEL), jnp.float32)
    offs = jax.random.randint(next(ks), (BATCH, 1), 0, 1024, dtype=jnp.int32)
    positions = (jnp.arange(SEQ, dtype=jnp.int32)[None, :] + offs).astype(jnp.int32)
    return {
        "x": x,
        "positions": positions,
        "ffn_pre_g": g((DEPTH, 2, D_MODEL)),
        "ffn_post_g": g((DEPTH, 2, D_MODEL)),
        "ffn_w_gate": w((DEPTH, 2, D_MODEL, D_FF), D_MODEL),
        "ffn_w_up": w((DEPTH, 2, D_MODEL, D_FF), D_MODEL),
        "ffn_w_down": w((DEPTH, 2, D_FF, D_MODEL), D_FF),
        "mix_pre_g": g((DEPTH, D_MODEL)),
        "mix_post_g": g((DEPTH, D_MODEL)),
        "gmlp_w_in": w((N_A_LAYERS, D_MODEL, 2 * GMLP_HALF), D_MODEL),
        "gmlp_ln_g": g((N_A_LAYERS, GMLP_HALF)),
        "gmlp_ln_b": 0.02 * jax.random.normal(next(ks), (N_A_LAYERS, GMLP_HALF), jnp.float32),
        "gmlp_w_s": w((N_A_LAYERS, GMLP_GROUPS, CHUNK, CHUNK), CHUNK),
        "gmlp_b_s": g((N_A_LAYERS, GMLP_GROUPS, CHUNK)),
        "gmlp_w_out": w((N_A_LAYERS, GMLP_HALF, D_MODEL), GMLP_HALF),
        "kv_norm_g": g((D_MODEL,)),
        "w_dkv": w((D_MODEL, KV_RANK + QK_ROPE), D_MODEL),
        "kv_a_norm_g": g((KV_RANK,)),
        "w_ukv": w((KV_RANK, N_HEADS * (QK_NOPE + V_DIM)), KV_RANK),
        "mla_w_dq": w((N_B_LAYERS, D_MODEL, Q_RANK), D_MODEL),
        "mla_q_norm_g": g((N_B_LAYERS, Q_RANK)),
        "mla_w_uq": w((N_B_LAYERS, Q_RANK, N_HEADS * (QK_NOPE + QK_ROPE)), Q_RANK),
        "mla_w_o": w((N_B_LAYERS, N_HEADS * V_DIM, D_MODEL), N_HEADS * V_DIM),
    }

def first_block(x, positions, ffn_pre_g, ffn_post_g, ffn_w_gate, ffn_w_up, ffn_w_down,
              mix_pre_g, mix_post_g, gmlp_w_in, gmlp_ln_g, gmlp_ln_b, gmlp_w_s, gmlp_b_s,
              gmlp_w_out, kv_norm_g, w_dkv, kv_a_norm_g, w_ukv, mla_w_dq, mla_q_norm_g,
              mla_w_uq, mla_w_o):
    cos, sin = rope_tables(positions)
    h = x
    k_nope = k_rope = v = None
    for layer in range(DEPTH):
        f = swiglu(rms_norm(h, ffn_pre_g[layer, 0]), ffn_w_gate[layer, 0], ffn_w_up[layer, 0], ffn_w_down[layer, 0])
        h = h + 0.5 * rms_norm(f, ffn_post_g[layer, 0])
        n = rms_norm(h, mix_pre_g[layer])
        if layer < N_A_LAYERS:
            m = gmlp_mixer(n, gmlp_w_in[layer], gmlp_ln_g[layer], gmlp_ln_b[layer],
                           gmlp_w_s[layer], gmlp_b_s[layer], gmlp_w_out[layer])
        else:
            j = layer - N_A_LAYERS
            m = mla_mixer(n, k_nope, k_rope, v, mla_w_dq[j], mla_q_norm_g[j], mla_w_uq[j], mla_w_o[j], cos, sin)
        h = h + rms_norm(m, mix_post_g[layer])
        f = swiglu(rms_norm(h, ffn_pre_g[layer, 1]), ffn_w_gate[layer, 1], ffn_w_up[layer, 1], ffn_w_down[layer, 1])
        h = h + 0.5 * rms_norm(f, ffn_post_g[layer, 1])
        if layer == N_A_LAYERS - 1:
            k_nope, k_rope, v = shared_kv(h, kv_norm_g, w_dkv, kv_a_norm_g, w_ukv, cos, sin)
    return h


DEPTH_2 = 1

HEAD_DIM = 64
N_HEADS_FOX = 8
N_HEADS_DSA = 8
N_IDX_HEADS = 8
IDX_DIM = 64
TOPK_MAX = 256
N_BUCKETS = 32
MAX_DISTANCE = 128
EPS = 1e-6
NEG_INF_2 = -1e30

FOX_W = N_HEADS_FOX * HEAD_DIM
DSA_W = N_HEADS_DSA * HEAD_DIM
IDX_Q_W = N_IDX_HEADS * IDX_DIM
IN_SPLITS = (FOX_W, FOX_W, FOX_W, N_HEADS_FOX,
             DSA_W, HEAD_DIM, HEAD_DIM,
             IDX_Q_W, IDX_DIM, N_IDX_HEADS,
             D_MODEL, D_MODEL)
IN_WIDTH = 3 * FOX_W + N_HEADS_FOX + DSA_W + 2 * HEAD_DIM + IDX_Q_W + IDX_DIM + N_IDX_HEADS + 2 * D_MODEL


def rms_norm_2(x, g):
    xf = x.astype(jnp.float32)
    y = xf * lax.rsqrt(jnp.mean(xf * xf, axis=-1, keepdims=True) + EPS)
    return (y * g.astype(jnp.float32)).astype(x.dtype)

def swiglu_ffn(x, g, w_gate, w_up, w_down):
    h = rms_norm_2(x, g)
    return (jax.nn.silu(h @ w_gate) * (h @ w_up)) @ w_down

def t5_causal_bucket(rel):
    max_exact = N_BUCKETS // 2
    relf = jnp.maximum(rel, 1).astype(jnp.float32)
    large = max_exact + (jnp.log(relf / max_exact) / math.log(MAX_DISTANCE / max_exact)
                         * (N_BUCKETS - max_exact)).astype(jnp.int32)
    large = jnp.minimum(large, N_BUCKETS - 1)
    return jnp.where(rel < max_exact, rel, large)

def split_columns(z):
    outs, off = [], 0
    for w in IN_SPLITS:
        outs.append(z[..., off:off + w])
        off += w
    return outs

def fox_attention(q, k, v, log_f):
    S = q.shape[1]
    cum = jnp.cumsum(log_f, axis=1).transpose(0, 2, 1)
    scale = HEAD_DIM ** -0.5
    outs = []
    for start in range(0, S, Q_BLOCK):
        end = start + Q_BLOCK
        logits = jnp.einsum('bqhd,bkhd->bhqk', q[:, start:end], k[:, :end]).astype(jnp.float32) * scale
        logits = logits + cum[:, :, start:end, None] - cum[:, :, None, :end]
        qpos = jnp.arange(start, end)[:, None]
        kpos = jnp.arange(end)[None, :]
        logits = jnp.where(kpos <= qpos, logits, NEG_INF_2)
        p = jax.nn.softmax(logits, axis=-1).astype(v.dtype)
        outs.append(jnp.einsum('bhqk,bkhd->bqhd', p, v[:, :end]))
    return jnp.concatenate(outs, axis=1)

def dsa_attention(q, k, v, q_idx, k_idx, w_idx, rel_bias):
    S = q.shape[1]
    topk = min(TOPK_MAX, S // 4)
    scale = HEAD_DIM ** -0.5
    idx_scale = IDX_DIM ** -0.5
    w = w_idx.astype(jnp.float32) * (N_IDX_HEADS ** -0.5)
    gather = jax.vmap(lambda arr, ind: arr[ind])
    outs = []
    for start in range(0, S, Q_BLOCK):
        end = start + Q_BLOCK
        n_keys = min(S, max(end, topk))
        qpos = jnp.arange(start, end)
        kpos = jnp.arange(n_keys)
        causal = kpos[None, :] <= qpos[:, None]
        s_idx = jax.nn.relu(jnp.einsum('bqhd,bkd->bqhk', q_idx[:, start:end],
                                       k_idx[:, :n_keys]).astype(jnp.float32) * idx_scale)
        score = jnp.einsum('bqhk,bqh->bqk', s_idx, w[:, start:end])
        score = jnp.where(causal[None], score, NEG_INF_2)
        _, sel = lax.top_k(score, topk)
        valid = sel <= qpos[None, :, None]
        k_sel = gather(k, sel)
        v_sel = gather(v, sel)
        logits = jnp.einsum('bqhd,bqkd->bhqk', q[:, start:end], k_sel).astype(jnp.float32) * scale
        bucket = t5_causal_bucket(jnp.maximum(qpos[None, :, None] - sel, 0))
        bias = rel_bias.astype(jnp.float32)[bucket]
        logits = logits + bias.transpose(0, 3, 1, 2)
        logits = jnp.where(valid[:, None], logits, NEG_INF_2)
        p = jax.nn.softmax(logits, axis=-1).astype(v.dtype)
        outs.append(jnp.einsum('bhqk,bqkd->bqhd', p, v_sel))
    return jnp.concatenate(outs, axis=1)

def second_inputs(seed: int = 0) -> dict:
    key = jax.random.key(seed)
    ks = jax.random.split(key, 24)
    f32 = jnp.float32

    def dense(k, fan_in, fan_out):
        return jax.random.normal(k, (fan_in, fan_out), f32) * fan_in ** -0.5

    def gain(k, n):
        return 1.0 + 0.02 * jax.random.normal(k, (n,), f32)

    return {
        "x": jax.random.normal(ks[0], (BATCH, SEQ, D_MODEL), f32),
        "ffn1_norm": gain(ks[1], D_MODEL),
        "ffn1_w_gate": dense(ks[2], D_MODEL, D_FF),
        "ffn1_w_up": dense(ks[3], D_MODEL, D_FF),
        "ffn1_w_down": dense(ks[4], D_FF, D_MODEL),
        "mix_norm": gain(ks[5], D_MODEL),
        "w_in": dense(ks[6], D_MODEL, IN_WIDTH),
        "b_forget": 1.0 + 0.1 * jax.random.normal(ks[7], (N_HEADS_FOX,), f32),
        "fox_q_norm": gain(ks[8], HEAD_DIM),
        "fox_k_norm": gain(ks[9], HEAD_DIM),
        "dsa_q_norm": gain(ks[10], HEAD_DIM),
        "dsa_k_norm": gain(ks[11], HEAD_DIM),
        "rel_bias": 0.5 * jax.random.normal(ks[12], (N_BUCKETS, N_HEADS_DSA), f32),
        "w_branch_a": dense(ks[13], FOX_W, D_MODEL),
        "w_branch_b": dense(ks[14], DSA_W, D_MODEL),
        "w_out": dense(ks[15], D_MODEL, D_MODEL),
        "ffn2_norm": gain(ks[16], D_MODEL),
        "ffn2_w_gate": dense(ks[17], D_MODEL, D_FF),
        "ffn2_w_up": dense(ks[18], D_MODEL, D_FF),
        "ffn2_w_down": dense(ks[19], D_FF, D_MODEL),
    }

def second_block(x, ffn1_norm, ffn1_w_gate, ffn1_w_up, ffn1_w_down, mix_norm, w_in, b_forget,
              fox_q_norm, fox_k_norm, dsa_q_norm, dsa_k_norm, rel_bias,
              w_branch_a, w_branch_b, w_out, ffn2_norm, ffn2_w_gate, ffn2_w_up, ffn2_w_down):
    B, S, _ = x.shape
    for _layer in range(DEPTH_2):
        x = x + 0.5 * swiglu_ffn(x, ffn1_norm, ffn1_w_gate, ffn1_w_up, ffn1_w_down)

        h = rms_norm_2(x, mix_norm)
        (fq, fk, fv, ff, dq, dk, dv, iq, ik, iw, ga, gb) = split_columns(h @ w_in)

        fq = rms_norm_2(fq.reshape(B, S, N_HEADS_FOX, HEAD_DIM), fox_q_norm)
        fk = rms_norm_2(fk.reshape(B, S, N_HEADS_FOX, HEAD_DIM), fox_k_norm)
        fv = fv.reshape(B, S, N_HEADS_FOX, HEAD_DIM)
        log_f = jax.nn.log_sigmoid((ff + b_forget).astype(jnp.float32))
        o_a = fox_attention(fq, fk, fv, log_f).reshape(B, S, FOX_W)

        dq = rms_norm_2(dq.reshape(B, S, N_HEADS_DSA, HEAD_DIM), dsa_q_norm)
        dk = rms_norm_2(dk, dsa_k_norm)
        iq = iq.reshape(B, S, N_IDX_HEADS, IDX_DIM)
        o_b = dsa_attention(dq, dk, dv, iq, ik, iw, rel_bias).reshape(B, S, DSA_W)

        merged = jax.nn.sigmoid(ga) * (o_a @ w_branch_a) + jax.nn.sigmoid(gb) * (o_b @ w_branch_b)
        x = x + merged @ w_out

        x = x + 0.5 * swiglu_ffn(x, ffn2_norm, ffn2_w_gate, ffn2_w_up, ffn2_w_down)
    return x


def setup_inputs(seed=0):
    out = dict(first_inputs(seed))
    for name, value in second_inputs(seed + 1).items():
        if name != "x":
            out[name + "_2"] = value
    return out


def reference(
    x, positions, ffn_pre_g, ffn_post_g, ffn_w_gate, ffn_w_up, ffn_w_down, mix_pre_g,
    mix_post_g, gmlp_w_in, gmlp_ln_g, gmlp_ln_b, gmlp_w_s, gmlp_b_s, gmlp_w_out, kv_norm_g,
    w_dkv, kv_a_norm_g, w_ukv, mla_w_dq, mla_q_norm_g, mla_w_uq, mla_w_o, ffn1_norm_2,
    ffn1_w_gate_2, ffn1_w_up_2, ffn1_w_down_2, mix_norm_2, w_in_2, b_forget_2, fox_q_norm_2,
    fox_k_norm_2, dsa_q_norm_2, dsa_k_norm_2, rel_bias_2, w_branch_a_2, w_branch_b_2, w_out_2,
    ffn2_norm_2, ffn2_w_gate_2, ffn2_w_up_2, ffn2_w_down_2,
):
    x = first_block(
        x, positions, ffn_pre_g, ffn_post_g, ffn_w_gate, ffn_w_up, ffn_w_down, mix_pre_g,
        mix_post_g, gmlp_w_in, gmlp_ln_g, gmlp_ln_b, gmlp_w_s, gmlp_b_s, gmlp_w_out, kv_norm_g,
        w_dkv, kv_a_norm_g, w_ukv, mla_w_dq, mla_q_norm_g, mla_w_uq, mla_w_o,
    )
    return second_block(
        x, ffn1_norm_2, ffn1_w_gate_2, ffn1_w_up_2, ffn1_w_down_2, mix_norm_2, w_in_2,
        b_forget_2, fox_q_norm_2, fox_k_norm_2, dsa_q_norm_2, dsa_k_norm_2, rel_bias_2,
        w_branch_a_2, w_branch_b_2, w_out_2, ffn2_norm_2, ffn2_w_gate_2, ffn2_w_up_2,
        ffn2_w_down_2,
    )


_drawn_inputs = setup_inputs


def setup_inputs(seed=0):
    import zlib

    import numpy as np

    out = dict(_drawn_inputs(seed))
    spreads = {}
    factors = {'ffn_post_g': 3.542,
     'mix_pre_g': 2.792,
     'gmlp_ln_g': 6.138,
     'gmlp_ln_b': 6.276,
     'gmlp_b_s': 4.107,
     'kv_norm_g': 4.412,
     'kv_a_norm_g': 4.65,
     'mla_q_norm_g': 8.0,
     'ffn1_norm_2': 8.0,
     'mix_norm_2': 6.732,
     'b_forget_2': 8.0,
     'fox_q_norm_2': 8.0,
     'fox_k_norm_2': 8.0,
     'dsa_q_norm_2': 8.0,
     'dsa_k_norm_2': 8.0,
     'ffn2_norm_2': 22.195,
     'rel_bias_2': 5.154}
    for name, (base, spread) in spreads.items():
        noise = np.random.default_rng([zlib.crc32(name.encode()), seed]).standard_normal(out[name].shape)
        drawn = base * np.exp(spread * noise) if base else spread * noise
        out[name] = __import__('jax').numpy.asarray(drawn.astype(out[name].dtype))
    for name, factor in factors.items():
        out[name] = (out[name] * factor).astype(out[name].dtype)
    return out
```

```python
import math
from contextlib import ExitStack

import numpy as np

import concourse.bass as bass
import concourse.mybir as mybir

F32 = mybir.dt.float32
F32R = mybir.dt.float32r
I32 = mybir.dt.int32
ALU = mybir.AluOpType
ACT = mybir.ActivationFunctionType
AX = mybir.AxisListType

P = 128
NB = 2
TOK = NB * P
D = 1024
KT = D // P
BANK = 512
UNIT = 1024
RAW = 5
SPLIT = 10
N_ACC = 6
EPS = 1e-6
LN_EPS = 1e-5
NEG = -1e30
TAKEN = -3e38
SQ2PI = math.sqrt(2.0 / math.pi)


class Program:

    def __init__(self, nc, ctx):
        self.nc, self.ctx = nc, ctx
        self.queue = {"pe": [], "act": [], "dve": [], "pool": [], "sp": []}
        self.sems, self.count = {}, {}
        self.waited = {e: {} for e in self.queue}
        self.last = {}

    def op(self, engine, sem, fn, wait=(), inc=1):
        need = {}
        for token in wait:
            if token is not None and self.waited[engine].get(token[0], 0) < token[1]:
                need[token[0]] = max(need.get(token[0], 0), token[1])
        self.waited[engine].update(need)
        if sem is not None and sem not in self.sems:
            self.sems[sem] = self.ctx.enter_context(self.nc.semaphore(sem))
            self.count[sem] = 0
        self.queue[engine].append((need, fn, sem, inc))
        if sem is None:
            return None
        self.count[sem] += inc
        token = (sem, self.count[sem])
        if engine != "sp":
            self.last[engine, inc == 16] = token
        return token

    def pe(self, sem, fn, wait=()):
        return self.op("pe", sem, fn, wait)

    def act(self, sem, fn, wait=()):
        return self.op("act", sem, fn, wait)

    def dve(self, sem, fn, wait=()):
        return self.op("dve", sem, fn, wait)

    def pool(self, sem, fn, wait=()):
        return self.op("pool", sem, fn, [*wait, self.last.get(("pool", False))])

    def load(self, sem, out, in_, wait=(), engine="pool", **kw):
        return self.op(engine, sem, lambda e: e.dma_start(out, in_, **kw), wait, 16)

    def so_far(self):
        return list(self.last.values())

    def play(self, engine, e):
        for need, fn, sem, inc in self.queue[engine]:
            for name, value in need.items():
                e.wait_ge(self.sems[name], value)
            ins = fn(e)
            if sem is not None:
                ins.then_inc(self.sems[sem], inc)


def mm(out, lhsT, rhs, start, stop):
    return lambda e: e.matmul(out, lhsT, rhs, start=start, stop=stop, skip_group_check=True)


def tr(out, in_, ident):
    return lambda e: e.transpose(out, in_, ident)


def act(out, in_, func, **kw):
    return lambda e: e.activation(out, in_, func, **kw)


def tt(out, a, b, op):
    return lambda e: e.tensor_tensor(out, a, b, op)


def ts(out, a, s1, op0, s2=None, op1=None):
    if op1 is None:
        return lambda e: e.tensor_scalar(out, a, s1, None, op0)
    return lambda e: e.tensor_scalar(out, a, s1, s2, op0, op1)


def stt(out, a, s, op0, b, op1):
    return lambda e: e.scalar_tensor_tensor(out=out, in0=a, scalar=s, in1=b, op0=op0, op1=op1)


def copy(out, in_):
    return lambda e: e.tensor_copy(out, in_)


class Split:

    def __init__(self, hi, lo):
        self.hi, self.lo = hi, lo
        self.ready = {}
        self.read = [None, None]

    def parts(self, kt, b):
        cols = slice(b * P, (b + 1) * P)
        return self.hi[:, kt, cols], self.lo[:, kt, cols]


class Banks:

    def __init__(self, ids):
        self.ids, self.at = list(ids), 0
        self.free = {i: () for i in ids}

    def find(self, n):
        starts = [k for k in range(0, len(self.ids) - n + 1, n)]
        starts = [k for k in starts if k >= self.at] + [k for k in starts if k < self.at]
        for k in starts:
            if all(self.free[i] is not None for i in self.ids[k:k + n]):
                return k
        return None

    def available(self, n=1):
        return self.find(n) is not None

    def take(self, n=1):
        k = self.find(n)
        assert k is not None
        self.at = (k + n) % len(self.ids)
        tokens = []
        for i in self.ids[k:k + n]:
            tokens += self.free[i]
            self.free[i] = None
        return self.ids[k], tokens

    def take_pair(self):
        return self.take(2)


class Weights:

    def __init__(self, prog, raw, hi, lo):
        self.p, self.raw, self.hi, self.lo = prog, raw, hi, lo
        self.units, self.dma, self.split, self.used = [], [], [], []

    def plan(self, sources, widths):
        self.units.append((sources, widths))
        return len(self.units) - 1

    def shape(self, j):
        (sources, widths) = self.units[j]
        return sources[0].shape[1], sum(widths)

    def parts(self, j):
        a, w = self.shape(j)
        return [t[:, j % SPLIT, 0:a * w].rearrange("p (a w) -> p a w", a=a) for t in (self.hi, self.lo)]

    def load_next(self):
        j = len(self.dma)
        sources, widths = self.units[j]
        a, w = self.shape(j)
        dst = self.raw[:, j % RAW, 0:a * w].rearrange("p (a w) -> p a w", a=a)
        wait = [self.split[j - RAW]] if j >= RAW else []
        at = 0
        for src, width in zip(sources, widths):
            token = self.p.op("sp", f"w_raw{j % RAW}", lambda e, o=dst[:, :, at:at + width], i=src: e.dma_start(o, i),
                              wait, 16)
            at += width
        self.dma.append(token)

    def split_next(self):
        j = len(self.split)
        a, w = self.shape(j)
        raw = self.raw[:, j % RAW, 0:a * w]
        hi, lo = self.hi[:, j % SPLIT, 0:a * w], self.lo[:, j % SPLIT, 0:a * w]
        free = [self.used[j - SPLIT]] if j >= SPLIT else []
        t = self.p.act("w_hi", act(hi, raw, ACT.Copy), [self.dma[j], *free])
        self.split.append(self.p.dve("w_lo", tt(lo, raw, hi.bitcast(F32), ALU.subtract), [self.dma[j], t]))

    def pump(self, limit=SPLIT):
        until = len(self.split) + limit
        while True:
            j = len(self.split)
            if len(self.dma) < min(len(self.units), j + RAW):
                self.load_next()
            elif j < min(until, len(self.units)) and (j < SPLIT or len(self.used) > j - SPLIT):
                self.split_next()
            else:
                return

    def done(self, j, token):
        assert j == len(self.used)
        self.used.append(token)


def t5_buckets(rel, n_buckets=32, max_distance=128):
    exact = n_buckets // 2
    relf = np.maximum(rel, 1).astype(np.float32)
    large = exact + (np.log(relf / exact) / math.log(max_distance / exact) * (n_buckets - exact)).astype(np.int32)
    return np.where(rel < exact, rel, np.minimum(large, n_buckets - 1))


def constants():
    i = np.arange(P)
    later = (i[None, :] > i[:, None]).astype(np.float32)
    packed = np.concatenate([
        np.eye(P),
        np.eye(P)[::-1],
        np.zeros((P, P)), later * NEG,
        1.0 - later.T,
        np.ones((P, P)),
    ], axis=1).astype(np.float32)
    inv_freq = (np.float32(10000.0) ** (-np.arange(0, 64, 2, dtype=np.float32) / np.float32(64))).astype(np.float32)
    j = np.arange(384)
    onehot = (t5_buckets(np.maximum(255 - j, 0))[None, :] == np.arange(32)[:, None]).astype(np.float32)
    return {"c_packed": packed, "c_inv_freq": np.tile(inv_freq, (P, 1)), "c_onehot": onehot}


def gain_plan(d):
    at, plan = 0, []
    for name in ("ffn_pre_g", "mix_pre_g", "kv_norm_g", "kv_a_norm_g", "mla_q_norm_g", "ffn1_norm_2",
                 "mix_norm_2", "ffn2_norm_2", "gmlp_b_s"):
        size = 1
        for s in d[name].shape:
            size *= s
        plan.append((name, at, size // P))
        at += size // P
    return plan, at


def build(nc, d, out, stop_after=99):
    ctx = ExitStack()
    with ctx:
        prog = Program(nc, ctx)

        def sb(name, shape, dt=F32, scope=None):
            return (scope or ctx).enter_context(nc.sbuf_tensor(name, shape, dt))

        ps_all = ctx.enter_context(nc.psum_tensor("ps", [P, 8 * BANK], F32))

        def bank(i, a=0, n=BANK):
            return ps_all[:, i * BANK + a:i * BANK + a + n]

        acc = Banks(range(N_ACC))
        tbank = Banks(range(N_ACC, 8))

        w_raw = sb("w_raw", [P, RAW, UNIT])
        w_hi = sb("w_hi", [P, SPLIT, UNIT], F32R)
        w_lo = sb("w_lo", [P, SPLIT, UNIT], F32R)
        h = sb("h", [P, NB, D])
        work = sb("work", [P, NB, D])
        nT = Split(sb("nT_hi", [P, KT, TOK], F32R), sb("nT_lo", [P, KT, TOK], F32R))
        post_g = sb("post_g", [P, D])
        gained = sb("gained", [P, 2, BANK])
        cst = sb("cst", [P, 6 * P])
        stat = sb("stat", [P, NB, 64])
        half = sb("half", [P, 9])
        plan, n_rows = gain_plan(d)
        gcol = sb("gcol", [P, n_rows])
        row_of = {name: r for name, r, _ in plan}
        rope = sb("rope", [P, NB, 2, 32])
        ident, flip, mask = cst[:, 0:P], cst[:, P:2 * P], cst[:, 2 * P:4 * P]
        upto, ones = cst[:, 4 * P:5 * P], cst[:, 5 * P:6 * P]

        bias_dram = nc.dram_tensor("bias_rows", [8, 384], F32, kind="Internal").ap()

        W = Weights(prog, w_raw, w_hi, w_lo)

        def plan_cols(w, ranges):
            width = sum(b - a for a, b in ranges)
            kts = w.shape[0] // P
            per = max(1, min(UNIT // width, kts))
            wv = w.rearrange("(c p) n -> p c n", p=P)
            units = []
            for k0 in range(0, kts, per):
                k1 = min(kts, k0 + per)
                j = W.plan([wv[:, k0:k1, a:b] for a, b in ranges], [b - a for a, b in ranges])
                units.append((j, list(range(k0, k1))))
            return units

        class Group:

            def __init__(self, consumer):
                self.units, self.pieces, self.consumer = [], {}, consumer

            def add(self, units, cols, x=None):
                for j, kts in units:
                    self.units.append(j)
                    self.pieces[j] = [(kt, i, c, n, name, x) for i, kt in enumerate(kts) for c, n, name in cols]
                return self

        def product3(dst, x, w, start, stop, wait):
            prog.pe(None, mm(dst, x[0], w[0], start, False), wait)
            prog.pe(None, mm(dst, x[0], w[1], False, False))
            return mm(dst, x[1], w[0], False, stop)

        background = []

        def step_background(b=None):
            for item in list(background):
                if b is None or item[0] == b:
                    try:
                        next(item[1])
                    except StopIteration:
                        background.remove(item)

        def finish(b=None):
            tries = 0
            while any(b is None or item[0] == b for item in background):
                step_background(b if tries % 16 < 15 else None)
                tries += 1

        def run_group(g, xT, lag=None, calm=False):
            n = len(g.units)
            lag = n if lag is None else min(lag, n)
            order = []
            for i in range(n + lag):
                if i < n:
                    order.append((0, i))
                if i >= lag:
                    order.append((1, i - lag))
            total = {}
            for j in g.units:
                for piece in g.pieces[j]:
                    total[piece[4]] = total.get(piece[4], 0) + 1
            banks, seen, done = [{}, {}], [{}, {}], [{}, {}]
            for b, i in order:
                if i == 0:
                    finish(b)
                j = g.units[i]
                if len(W.split) <= j:
                    W.pump(1)
                whi, wlo = W.parts(j)
                for piece in g.pieces[j]:
                    kt, a, c, width, name, x = piece
                    x = x or xT
                    while (kt, b) not in x.ready:
                        step_background()
                    if name not in banks[b]:
                        while not acc.available():
                            step_background()
                        banks[b][name], free = acc.take()
                    else:
                        free = ()
                    k = seen[b].get(name, 0)
                    seen[b][name] = k + 1
                    last = k + 1 == total[name]
                    fn = product3(bank(banks[b][name], 0, width), x.parts(kt, b),
                                  (whi[:, a, c:c + width], wlo[:, a, c:c + width]), k == 0, last,
                                  [W.split[j], x.ready[kt, b], *free])
                    end_of_unit = piece is g.pieces[j][-1]
                    token = prog.pe("pe_unit" if last or end_of_unit else None, fn)
                    if last:
                        done[b][name] = token
                x.read[b] = token
                if b == 1:
                    W.done(j, token)
                if i == n - 1:
                    background.append((b, g.consumer(b, banks[b], done[b])))
                step_background()
                W.pump(i % 2 if calm and b == 1 and i >= n - lag else 1)

        def rms_scale(b, col, sources, n, sem, wait, junk=None):
            junk = work[:, b, :] if junk is None else junk
            root = 1.0 / math.sqrt(n)
            exact = root == 2.0 ** round(math.log2(root))
            at, token, c = 0, None, 0
            for src in sources:
                width = src.shape[1]
                token = prog.act(sem + "_sq", act(junk[:, at:at + width], src, ACT.Square,
                                                  scale=root if exact else 1.0, accum_out=stat[:, b, col + c:col + c + 1]),
                                 wait)
                at += width
                c += 1
            s, t = stat[:, b, col:col + 1], stat[:, b, col + 2:col + 3]
            if c == 2:
                token = prog.dve(sem + "_ms", ts(t, s, stat[:, b, col + 1:col + 2], ALU.add, EPS, ALU.add), [token])
            elif exact:
                token = prog.dve(sem + "_ms", ts(t, s, EPS, ALU.add), [token])
            else:
                token = prog.dve(sem + "_ms", ts(t, s, 1.0 / n, ALU.mult, EPS, ALU.add), [token])
            return t, prog.pool(sem + "_rs", tt(t, t, half[:, 0:1], ALU.pow), [token, half_ready[0]])

        def transpose(tiles, wait):
            i, free = tbank.take()
            for n, t in enumerate(tiles):
                w = t.shape[1]
                token = prog.pe("pe_tr", tr(bank(i, n * P, P)[0:w, :], t, ident), [*wait, *free])
            return i, token

        def evacuate_split(i, n, dst, kt0, b, wait, scale=1.0, owner=None):
            src = bank(i, 0, n * P).rearrange("p (c t) -> p c t", c=n)
            hi, lo = (x[:, kt0:kt0 + n, b * P:(b + 1) * P] for x in (dst.hi, dst.lo))
            t = prog.act("tr_hi", act(hi, src, ACT.Copy, scale=scale), [*wait, dst.read[b]])
            t = prog.dve("tr_lo", stt(lo, src, scale, ALU.mult, hi.bitcast(F32), ALU.subtract), [t])
            (owner or tbank).free[i] = (t,)
            for c in range(n):
                dst.ready[kt0 + c, b] = t

        def evacuate_gained(i, n, row, dst, kt0, b, wait):
            src = bank(i, 0, n * P).rearrange("p (c t) -> p c t", c=n)
            slot = gained_use[0] % 2
            gained_use[0] += 1
            g = gained[:, slot, 0:n * P].rearrange("p (c t) -> p c t", c=n)
            gain = gcol[:, row:row + n].unsqueeze(2).broadcast_to([P, n, P])
            hi, lo = (x[:, kt0:kt0 + n, b * P:(b + 1) * P] for x in (dst.hi, dst.lo))
            t = prog.dve("gain", tt(g, src, gain, ALU.mult), [*wait, gain_ready[0], gained_free[slot]])
            tbank.free[i] = (t,)
            t = prog.act("gain_hi", act(hi, g, ACT.Copy), [t, dst.read[b]])
            t = prog.dve("gain_lo", tt(lo, g, hi.bitcast(F32), ALU.subtract), [t])
            gained_free[slot] = t
            for c in range(n):
                dst.ready[kt0 + c, b] = t

        gained_use, gained_free = [0], [None, None]
        gain_ready, half_ready, rope_ready, bias_stored = [None], [None], [None], [None]
        h_ready = [None, None]

        def r_(b):
            return stat[:, b, 4:5]

        def r_half(b):
            return stat[:, b, 5:6]

        def r_square_half(b):
            return stat[:, b, 6:7]

        r_ready = [None, None]

        def h_to_nT(b, row, wait):
            for q in range(2):
                i, t = transpose([h[:, b, (4 * q + c) * P:(4 * q + c + 1) * P] for c in range(4)], [wait[q]])
                evacuate_gained(i, 4, row + 4 * q, nT, 4 * q, b, [t])
                yield

        def measure(b, wait):
            t = prog.act("pre_sq", act(work[:, b, :], h[:, b, :], ACT.Square, scale=D ** -0.5, accum_out=r_half(b)),
                         [*wait])
            t = prog.dve("pre_ms", ts(r_half(b), r_half(b), EPS, ALU.add), [t])
            prog.pool("pre_r", tt(r_(b), r_half(b), half[:, 0:1], ALU.pow), [t, half_ready[0]])
            prog.pool("pre_r", tt(r_half(b), r_(b), half[:, 8:9], ALU.mult))
            r_ready[b] = prog.pool("pre_r", tt(r_square_half(b), r_half(b), r_(b), ALU.mult))

        def add_branch(row, coef, post):

            def consumer(b, banks, done):
                halves = [bank(banks["D0"]), bank(banks["D1"])]
                cols = [slice(q * BANK, (q + 1) * BANK) for q in range(2)]
                joined = []
                if post:
                    c0, c1, rs = (stat[:, b, c:c + 1] for c in range(3))
                    sq = [prog.act("post_sq", act(work[:, b, cols[q]], halves[q], ACT.Square, scale=D ** -0.5, accum_out=c),
                                   [done["D0"], done["D1"]]) for q, c in enumerate((c0, c1))]
                    t0 = prog.dve("post_gain", stt(halves[0], halves[0], coef, ALU.mult, post_g[:, cols[0]], ALU.mult),
                                  [sq[0], post_ready[0]])
                    t = prog.dve("post_ms", ts(rs, c0, c1, ALU.add, EPS, ALU.add), [sq[1]])
                    t = prog.pool("post_rs", tt(rs, rs, half[:, 0:1], ALU.pow), [t])
                    t1 = prog.dve("post_gain", stt(halves[1], halves[1], coef, ALU.mult, post_g[:, cols[1]], ALU.mult), [sq[1]])
                    post_read[b] = t1
                    yield
                    for q, tq in enumerate((t0, t1)):
                        joined.append(prog.dve("h_add", stt(h[:, b, cols[q]], halves[q], rs, ALU.mult, h[:, b, cols[q]], ALU.add), [t, tq]))
                        acc.free[banks[f"D{q}"]] = (joined[q],)
                else:
                    for q in range(2):
                        joined.append(prog.dve("h_add", stt(h[:, b, cols[q]], halves[q], coef, ALU.mult, h[:, b, cols[q]], ALU.add),
                                               [done["D0"], done["D1"]]))
                        acc.free[banks[f"D{q}"]] = (joined[q],)
                h_ready[b] = joined[1]
                yield
                if row is not None:
                    if post:
                        yield
                    yield from h_to_nT(b, row, joined)
                    measure(b, [joined[1]])

            return consumer

        post_ready, post_read = [None], [None, None]

        def load_post(gain):
            post_ready[0] = prog.load("post_load", post_g[:, :], gain.partition_broadcast(P), post_read)

        def plan_ffn(wg, wu, wd):
            F = wg.shape[1]
            slices = []
            for c0 in range(0, F, BANK):
                n = min(BANK, F - c0)
                slices.append((c0, n, plan_cols(wg, [(c0, c0 + n)]), plan_cols(wu, [(c0, c0 + n)])))
            return F, slices, plan_cols(wd, [(0, D)])

        def ffn(name, planned, row_next, coef, post):
            F, slices, down = planned
            with ExitStack() as scope:
                free = prog.so_far()
                hT = Split(sb(name + "_hT_hi", [P, F // P, TOK], F32R, scope), sb(name + "_hT_lo", [P, F // P, TOK], F32R, scope))
                th = sb(name + "_th", [P, NB, BANK], F32, scope)
                hs = sb(name + "_hs", [P, NB, BANK], F32, scope)
                for c0, n, ug, uu in slices:
                    def consumer(b, banks, done, c0=c0, n=n):
                        g, u = bank(banks["G"], 0, n), bank(banks["U"], 0, n)
                        t1 = prog.act("silu_th", act(th[:, b, 0:n], g, ACT.Tanh, scale=r_half(b)), [done["G"], r_ready[b], *free])
                        t2 = prog.dve("silu_a", stt(hs[:, b, 0:n], th[:, b, 0:n], 1.0, ALU.add, g, ALU.mult), [t1, *free])
                        acc.free[banks["G"]] = (t2,)
                        t3 = prog.dve("silu_b", stt(th[:, b, 0:n], hs[:, b, 0:n], r_square_half(b), ALU.mult, u, ALU.mult), [t2, done["U"]])
                        acc.free[banks["U"]] = (t3,)
                        yield
                        yield
                        yield
                        i, t = transpose([th[:, b, c:c + P] for c in range(0, n, P)], [t3])
                        yield
                        evacuate_split(i, n // P, hT, c0 // P, b, [t])

                    g = Group(consumer).add(ug, [(0, n, "G")]).add(uu, [(0, n, "U")])
                    run_group(g, nT, lag=None if c0 == 0 and name != "f0" else 5)
                    if c0 == 0 and post is not None:
                        load_post(post)
                g = Group(add_branch(row_next, coef, post is not None)).add(down, [(0, BANK, "D0"), (BANK, BANK, "D1")])
                run_group(g, hT, lag=7, calm=True)

        def gmlp(row_next):
            H, G = 2 * D, 16
            with ExitStack() as scope:
                free = prog.so_far()
                v = sb("g_v", [P, NB, H], F32, scope)
                wsT = sb("g_wsT", [P, G, P], F32, scope)
                yT = Split(sb("g_yT_hi", [P, H // P, TOK], F32R, scope), sb("g_yT_lo", [P, H // P, TOK], F32R, scope))
                bn = sb("g_bn", [P, NB, 4, 6], F32, scope)
                ws_nat = v[:, 0, :].rearrange("p (g c) -> p g c", g=G)
                ws_t = prog.load("ws_load", ws_nat, d["gmlp_w_s"][0].rearrange("g t c -> t g c"), free)
                ws_read, ws_ready, bsT_row = [], [], row_of["gmlp_b_s"]

                def prepare_ws():
                    for _ in range(7):
                        yield
                    for q in range(G // 4):
                        i, t = transpose([ws_nat[:, 4 * q + k, :] for k in range(4)], [ws_t])
                        ws_read.append(t)
                        t = prog.dve("ws_mask", tt(wsT[:, 4 * q:4 * q + 4, :], bank(i).rearrange("p (g t) -> p g t", g=4),
                                                   upto.unsqueeze(1).broadcast_to([P, 4, P]), ALU.mult), [t, *free])
                        tbank.free[i] = (t,)
                        ws_ready.append(t)
                        yield

                us = [work[:, :, 0:BANK], work[:, :, BANK:D]]
                ln_gb = [gained, post_g[:, :].rearrange("p (n c) -> p n c", n=2)]
                u_ready, u_read = [[None] * 4, [None] * 4], [[None] * 4, [None] * 4]

                def gelu2(b, xs, dsts, done, dst_wait, out):
                    t = [prog.act("gelu_sq", act(w, x, ACT.Square, scale=r_(b)), [*done, r_ready[b], *dst_wait, *free]) for w, x in zip(dsts, xs)]
                    yield
                    for n, (w, x) in enumerate(zip(dsts, xs)):
                        t[n] = prog.dve("gelu_p", ts(w, w, 0.044715, ALU.mult, 1.0, ALU.add), [t[n]])
                        t[n] = prog.dve("gelu_q", stt(w, w, r_(b), ALU.mult, x, ALU.mult), [t[n]])
                        t[n] = prog.act("gelu_th", act(w, w, ACT.Tanh, scale=SQ2PI), [t[n]])
                    yield
                    for n, (w, x) in enumerate(zip(dsts, xs)):
                        out.append(prog.dve("gelu_r", stt(w, w, 1.0, ALU.add, x, ALU.mult), [t[n]]))

                v_ready, ln_done = [None, None], [[None] * 4, [None] * 4]
                stats_ready = [[], []]

                def v_consumer(s0):
                    def consumer(b, banks, done):
                        while len(ws_read) < G // 4:
                            yield
                        names, made = [f"V{s}" for s in (s0, s0 + 1)], []
                        dsts = [v[:, b, s * BANK:(s + 1) * BANK] for s in (s0, s0 + 1)]
                        yield from gelu2(b, [bank(banks[n]) for n in names], dsts, [done[n] for n in names], ws_read, made)
                        for n, s in enumerate((s0, s0 + 1)):
                            acc.free[banks[names[n]]] = (made[n],)
                            stats_ready[b].append(prog.dve("ln_stats", lambda e, o=bn[:, b, s, :], i=dsts[n]: e.bn_stats(o, i), [made[n], *free]))
                        yield
                        if s0 == 2:
                            mv = stat[:, b, 8:10]
                            t = prog.dve("ln_aggr", lambda e, o=mv, i=bn[:, b, :, :]: e.bn_aggr(o, i), stats_ready[b])
                            t = prog.dve("ln_var", ts(stat[:, b, 10:11], stat[:, b, 9:10], r_square_half(b), ALU.mult, 0.5, ALU.mult), [t])
                            t = prog.dve("ln_var", ts(stat[:, b, 10:11], stat[:, b, 10:11], LN_EPS, ALU.add), [t])
                            t = prog.pool("ln_rs", tt(stat[:, b, 10:11], stat[:, b, 10:11], half[:, 0:1], ALU.pow), [t])
                            yield
                            t = prog.dve("ln_rs_half", ts(stat[:, b, 11:12], stat[:, b, 10:11], r_half(b), ALU.mult), [t])
                            v_ready[b] = prog.dve("ln_norm", ts(v[:, b, :], v[:, b, :], stat[:, b, 8:9], ALU.subtract,
                                                                stat[:, b, 11:12], ALU.mult), [t])
                    return consumer

                ln_loaded, ln_read = [None] * 4, [(), ()]

                def load_ln(s, wait):
                    cols = slice(s * BANK, (s + 1) * BANK)
                    ln_loaded[s] = [prog.load(f"ln_load{s % 2}", ln_gb[s % 2][:, n, :], d[name][0, cols].partition_broadcast(P), wait)
                                    for n, name in enumerate(("gmlp_ln_g", "gmlp_ln_b"))]

                def ln_affine():
                    for s in range(4):
                        cols, g_b = slice(s * BANK, (s + 1) * BANK), ln_gb[s % 2]
                        for b in range(NB):
                            while v_ready[b] is None:
                                yield
                            t = prog.pool("ln_gain", tt(v[:, b, cols], v[:, b, cols], g_b[:, 0, :], ALU.mult), [v_ready[b], *ln_loaded[s]])
                            ln_done[b][s] = prog.pool("ln_bias", tt(v[:, b, cols], v[:, b, cols], g_b[:, 1, :], ALU.add), [t])
                            yield
                        if s < 2:
                            load_ln(s + 2, [ln_done[0][s], ln_done[1][s]])
                        if s == 1:
                            for _ in range(6):
                                yield
                    post_read[:] = ln_done[0][3], ln_done[1][3]
                    load_post(d["mix_post_g"][0])

                def u_consumer(s0):
                    def consumer(b, banks, done):
                        names, made = [f"U{s}" for s in (s0, s0 + 1)], []
                        dsts = [us[n][:, b, :] for n in range(2)]
                        while s0 == 2 and u_read[b][1] is None:
                            yield
                        yield from gelu2(b, [bank(banks[n]) for n in names], dsts, [done[n] for n in names], u_read[b][0:2], made)
                        for n, u in enumerate(dsts):
                            acc.free[banks[names[n]]] = (made[n],)
                            u_ready[b][s0 + n] = prog.act("u_scale", act(u, u, ACT.Copy, scale=r_(b)), [made[n]])
                    return consumer

                def mix(b, s):
                    u = us[s % 2][:, b, :]
                    while u_ready[b][s] is None or ln_done[b][s] is None or not acc.available():
                        yield
                    i, sv_free = acc.take()
                    for k in range(4):
                        g = 4 * s + k
                        t = prog.pe("pe_mix", mm(bank(i, k * P, P), wsT[:, g, :], v[:, b, g * P:(g + 1) * P], True, True),
                                    [ln_done[b][s], ws_ready[g // 4], *sv_free])
                    yield
                    for k in range(4):
                        g = 4 * s + k
                        t = prog.dve("mix_bias_u", stt(u[:, k * P:(k + 1) * P], bank(i, k * P, P),
                                                       gcol[:, bsT_row + g:bsT_row + g + 1], ALU.add,
                                                       u[:, k * P:(k + 1) * P], ALU.mult), [t, u_ready[b][s]])
                    acc.free[i] = (t,)
                    for _ in range(6):
                        yield
                    j, t = transpose([u[:, k * P:(k + 1) * P] for k in range(4)], [t])
                    u_read[b][s] = t
                    yield
                    evacuate_split(j, 4, yT, 4 * s, b, [t], scale=0.5)

                def mix_all(b):
                    for s in range(4):
                        yield from mix(b, s)

                background.append((2, prepare_ws()))
                for s0 in (0, 2):
                    if s0 == 2:
                        background.append((2, ln_affine()))
                    g = Group(v_consumer(s0))
                    for s in (s0, s0 + 1):
                        g.add(gmlp_in[s], [(0, BANK, f"V{s}")])
                    run_group(g, nT, lag=None)
                    if s0 == 0:
                        load_ln(0, gained_free)
                        load_ln(1, post_read)
                for s0 in (0, 2):
                    if s0 == 2:
                        background.extend((2, mix_all(b)) for b in range(NB))
                    g = Group(u_consumer(s0))
                    for s in (s0, s0 + 1):
                        g.add(gmlp_in[4 + s], [(0, BANK, f"U{s}")])
                    run_group(g, nT, lag=None)
                g = Group(add_branch(row_next, 1.0, True)).add(gmlp_out, [(0, BANK, "D0"), (BANK, BANK, "D1")])
                run_group(g, yT, lag=7, calm=True)

        def rotate(x, dst, tmp, b, wait, dst_wait=()):
            H = x.shape[1]
            cos, sin = (rope[:, b, q, :].unsqueeze(1).broadcast_to([P, H, 32]) for q in range(2))
            tmp = tmp.rearrange("p (h r) -> p h r", h=H)
            x1, x2, o1, o2 = x[:, :, 0:32], x[:, :, 32:64], dst[:, :, 0:32], dst[:, :, 32:64]
            t = None
            for o, y, z, join in ((o1, x1, x2, ALU.subtract), (o2, x2, x1, ALU.add)):
                prog.dve(None, tt(o, y, cos, ALU.mult), [*wait, *dst_wait, rope_ready[0], t])
                t = prog.dve("rope_sin_part", tt(tmp, z, sin, ALU.mult), [t])
                t = prog.dve("rope_join", tt(o, o, tmp, join), [t])
            return t

        def attention(b, heads, slot, scores, v_of, rows, owner, put, free, scale=1.0, key_mask=None, late=None):
            nk = (b + 1) * P
            while not acc.available(b + 1):
                yield
            if b == 0:
                i, bfree = acc.take()
            else:
                i, bfree = acc.take_pair()
            s = ps_all[:, i * BANK:i * BANK + 4 * nk].rearrange("p (h k) -> p h k", h=4)
            p = att_p[0][:, slot, 0:4 * nk].rearrange("p (h k) -> p h k", h=4)
            pT = work[:, slot, :].rearrange("p (n q) -> p n q", q=P)
            used = (i,) if b == 0 else (i, i + 1)
            for k, h_ in enumerate(heads):
                t = scores(h_, s[:, k, :], bfree)
            m_ap, m_t = key_mask()
            m4 = m_ap.unsqueeze(1).broadcast_to([P, 4, nk])
            if scale == 1.0:
                t = prog.dve("att_mask", tt(p, s, m4, ALU.add), [t, m_t, p_free[slot], *free])
            else:
                t = prog.dve("att_mask", stt(p, s, scale, ALU.mult, m4, ALU.add), [t, m_t, p_free[slot], *free])
            for u in used:
                acc.free[u] = (t,)
            c0 = 16 + 16 * slot
            mx, ng, sm, ri = (stat[:, 0, c0 + 4 * q:c0 + 4 * q + 4] for q in range(4))
            t = prog.dve("att_max", lambda e, o=mx, x=p: e.reduce_max(o, x, axis=AX.X), [t])
            t = prog.dve("att_neg", ts(ng, mx, -1.0, ALU.mult), [t])
            if late is not None:
                t = late(b, heads, mx, ng, t)
            yield
            for k in range(4):
                t = prog.act("att_exp", act(p[:, k, :], p[:, k, :], ACT.Exp, bias=ng[:, k:k + 1], accum_out=sm[:, k:k + 1]), [t])
            t = prog.dve("att_recip", lambda e, o=ri, x=sm: e.reciprocal(o, x), [t])
            t = prog.dve("att_norm", tt(p, p, ri.unsqueeze(2).broadcast_to([P, 4, nk]), ALU.mult), [t])
            yield
            for kb in range(b + 1):
                j, t2 = transpose([p[:, k, kb * P:(kb + 1) * P] for k in range(4)], [t])
                e_ = prog.act if kb else prog.dve
                f_ = act(pT[:, 4 * kb:4 * kb + 4, :], bank(j).rearrange("p (k q) -> p k q", k=4), ACT.Copy) if kb else \
                    copy(pT[:, 4 * kb:4 * kb + 4, :], bank(j).rearrange("p (k q) -> p k q", k=4))
                t3 = e_("att_pT_a" if kb else "att_pT_d", f_, [t2, pT_free[slot], *free])
                tbank.free[j] = (t3,)
                if kb == 0:
                    first = t3
            p_free[slot] = t2
            yield
            while not acc.available():
                yield
            j, bfree = acc.take()
            for k, h_ in enumerate(heads):
                part, col = rows(h_, k)
                dst = bank(j, col * P, P)[part, :]
                for kb in range(b + 1):
                    t = prog.pe("pe_pv", mm(dst, v_of(h_, kb), pT[:, 4 * kb + k, :], kb == 0, kb == b), [first, t3, *bfree])
            pT_free[slot] = t
            put(j, t)
            yield

        att_p, p_free, pT_free = [None], [None, None], [None, None]

        def pipeline(gens):
            active, waiting = [], list(gens)
            while active or waiting:
                if waiting and len(active) < 2:
                    active.append(waiting.pop(0))
                for g in active[::-1]:
                    try:
                        next(g)
                    except StopIteration:
                        active.remove(g)
                W.pump()
                yield

        def put_split(dst, kt0, n, b):
            def put(j, t):
                evacuate_split(j, n, dst, kt0, b, [t], owner=acc)
            return put

        def shared_kv_down(row_next, cT, krT, scope):
            free = prog.so_far()
            nat = sb("kv_nat", [P, NB, BANK], F32, scope)

            def consumer(b, banks, done):
                c = nat[:, b, 0:320]
                tc = prog.act("kv_out", act(c, bank(banks["C"], 0, 320), ACT.Copy, scale=r_(b)), [done["C"], r_ready[b], *free])
                acc.free[banks["C"]] = (tc,)
                yield from h_to_nT(b, row_next, [h_ready[b]] * 2)
                t, token = rms_scale(b, 12, [c[:, 0:256]], 256, "kva", [tc], junk=work[:, b, 0:256])
                yield
                t1 = prog.dve("kv_norm", ts(nat[:, b, 0:256], c[:, 0:256], t, ALU.mult), [token])
                kr = work[:, b, 256:320].unsqueeze(1)
                t2 = rotate(c[:, 256:320].unsqueeze(1), kr, work[:, b, 320:352], b, [tc], free)
                t2 = prog.dve("kr_once", copy(nat[:, b, 256:320], work[:, b, 256:320]), [t2])
                t2 = prog.dve("kr_twice", copy(nat[:, b, 320:384], nat[:, b, 256:320]), [t2])
                yield
                i, t = transpose([nat[:, b, 0:128], nat[:, b, 128:256], nat[:, b, 256:384]], [t1, t2])
                t = prog.act("krT", act(krT[:, b * P:(b + 1) * P], bank(i, 256, P), ACT.Copy), [t, *free])
                krT_ready[b] = t
                evacuate_gained(i, 2, row_of["kv_a_norm_g"], cT, 0, b, [t, *free])

            g = Group(consumer).add(dkv, [(0, 320, "C")])
            run_group(g, nT)

        krT_ready = [None, None]

        def mla(row_next, cT, krT):
            with ExitStack() as scope:
                free = prog.so_far()
                kT = sb("m_kT", [P, 8, TOK], F32, scope)
                v = sb("m_v", [P, NB, D], F32, scope)
                qT = sb("m_qT", [P, 8, TOK], F32, scope)
                qrT = sb("m_qrT", [P, 8, TOK], F32, scope)
                qlT = Split(sb("m_ql_hi", [P, 4, TOK], F32R, scope), sb("m_ql_lo", [P, 4, TOK], F32R, scope))
                nat = sb("m_nat", [P, NB, BANK], F32, scope)
                att_p[0] = sb("m_p", [P, 2, D], F32, scope)
                zero = [prog.pool("q_zero", lambda e, x=x: e.memset(x, 0.0), free) for x in (qrT[64:128, 0::2, :], qrT[0:64, 1::2, :])]
                kT_ready, v_ready = [], [None, None]

                for half_, units in enumerate(ukv):
                    W.pump()
                    w = [W.parts(j) for j, _ in units]
                    wait = [W.split[j] for j, _ in units]
                    for pair in range(2):
                        i, bfree = acc.take()
                        for k in range(2):
                            c = (2 * pair + k) * 256
                            for kt in range(2):
                                x = tuple(a[:, 0, c:c + P] for a in w[kt])
                                fn = product3(bank(i, k * 256, 256), x, (cT.hi[:, kt, :], cT.lo[:, kt, :]), kt == 0, kt == 1,
                                              [*wait, cT.ready[kt, 0], cT.ready[kt, 1], *bfree])
                                t = prog.pe("pe_kv", fn)
                        h0 = 4 * half_ + 2 * pair
                        t = prog.act("kT_out", act(kT[:, h0:h0 + 2, :], bank(i).rearrange("p (h t) -> p h t", h=2), ACT.Copy), [t, *free])
                        acc.free[i] = (t,)
                        kT_ready.append(t)
                    for b in range(NB):
                        i, bfree = acc.take()
                        for kt in range(2):
                            wv = tuple(a[:, 0, :].rearrange("p (h c) -> p h c", h=4)[:, :, 128:256] for a in w[kt])
                            dst = bank(i).rearrange("p (h c) -> p h c", h=4)
                            t = prog.pe("pe_kv", product3(dst, cT.parts(kt, b), wv, kt == 0, kt == 1, [*wait, *bfree]))
                        last = t
                        t = prog.dve("v_out", copy(v[:, b, half_ * BANK:(half_ + 1) * BANK], bank(i)), [t, *free])
                        acc.free[i] = (t,)
                        v_ready[b] = t
                        step_background()
                    for j, _ in units:
                        W.done(j, last)
                W.pump()

                def consumer(b, banks, done):
                    t = prog.act("ql_out", act(nat[:, b, :], bank(banks["Q"]), ACT.Copy, scale=r_(b)), [done["Q"], r_ready[b], *free])
                    acc.free[banks["Q"]] = (t,)
                    t, token = rms_scale(b, 12, [nat[:, b, :]], BANK, "ql", [t])
                    yield
                    t = prog.dve("ql_norm", ts(nat[:, b, :], nat[:, b, :], t, ALU.mult), [token])
                    yield
                    i, t = transpose([nat[:, b, k * P:(k + 1) * P] for k in range(4)], [t])
                    nat_read[b] = t
                    evacuate_gained(i, 4, row_of["mla_q_norm_g"], qlT, 0, b, [t, *free])

                nat_read = [None, None]
                run_group(Group(consumer).add(dq_lat, [(0, BANK, "Q")]), nT)
                load_post(d["mix_post_g"][1])
                finish()

                qT_ready, qrT_ready = [], []
                for half_, units in enumerate(uq):
                    W.pump()
                    w = [W.parts(j) for j, _ in units]
                    wait = [W.split[j] for j, _ in units]
                    turned = []
                    for b in range(NB):
                        i, bfree = acc.take()
                        for kt in range(4):
                            wr = tuple(a[:, 0, 0:768].rearrange("p (h c) -> p h c", h=4)[:, :, 128:192] for a in w[kt])
                            dst = bank(i, 0, 256).rearrange("p (h c) -> p h c", h=4)
                            t = prog.pe("pe_q", product3(dst, qlT.parts(kt, b), wr, kt == 0, kt == 3, [*wait, qlT.ready[kt, b], *bfree]))
                        rot = nat[:, b, 0:256].rearrange("p (h c) -> p h c", h=4)
                        t = rotate(bank(i, 0, 256).rearrange("p (h c) -> p h c", h=4), rot, nat[:, b, 256:384], b, [t], [nat_read[b]])
                        acc.free[i] = (t,)
                        turned.append(t)
                    for pair in range(2):
                        i, bfree = acc.take()
                        for k in range(2):
                            c = (2 * pair + k) * 192
                            for kt in range(4):
                                x = tuple(a[:, 0, c:c + P] for a in w[kt])
                                fn = product3(bank(i, k * 256, 256), x, (qlT.hi[:, kt, :], qlT.lo[:, kt, :]), kt == 0, kt == 3, bfree)
                                t = prog.pe("pe_q", fn)
                        last = t
                        h0 = 4 * half_ + 2 * pair
                        t = prog.act("qT_out", act(qT[:, h0:h0 + 2, :], bank(i).rearrange("p (h t) -> p h t", h=2), ACT.Copy), [t, *free])
                        acc.free[i] = (t,)
                        qT_ready.append(t)
                    for j, _ in units:
                        W.done(j, last)
                    for b in range(NB):
                        i, t = transpose([nat[:, b, k * P:(k + 1) * P] for k in range(2)], [turned[b]])
                        nat_read[b] = t
                        src = bank(i, 0, 256).rearrange("p (c t) -> p c t", c=2)
                        for q in range(2):
                            rr = slice(64 * q, 64 * q + 64)
                            t = prog.act("qrT_out", act(qrT[rr, 4 * half_ + q:4 * half_ + 4:2, b * P:(b + 1) * P], src[rr, :, :], ACT.Copy),
                                         [t, *zero, *free])
                        tbank.free[i] = (t,)
                        qrT_ready.append(t)
                    W.pump()

                def scores(b):
                    blk, nk = slice(b * P, (b + 1) * P), (b + 1) * P

                    def queue(h_, out, bfree):
                        prog.pe(None, mm(out, qT[:, h_, blk], kT[:, h_, 0:nk], True, False), [qT_ready[-1], kT_ready[-1], *bfree])
                        return prog.pe("pe_score", mm(out, qrT[:, h_, blk], krT[:, 0:nk], False, True), [*qrT_ready, *krT_ready])
                    return queue

                att = [attention(b, range(4 * g, 4 * g + 4), n % 2, scores(b),
                                 lambda h_, kb: v[:, kb, h_ * P:(h_ + 1) * P], lambda h_, k: (slice(0, P), k),
                                 acc, put_split(nT, 4 * g, 4, b), [*free, *v_ready], scale=192.0 ** -0.5,
                                 key_mask=lambda b=b: (mask[:, P:2 * P] if b == 0 else mask, None))
                       for n, (b, g) in enumerate(((0, 0), (0, 1), (1, 0), (1, 1)))]
                for _ in pipeline(att):
                    pass
                g = Group(add_branch(row_next, 1.0, True)).add(w_o, [(0, BANK, "D0"), (BANK, BANK, "D1")])
                run_group(g, nT, lag=7, calm=True)

        def mixer2(row_next):
            outer = ExitStack()
            free0 = prog.so_far()
            oa = Split(sb("x_oa_hi", [P, 4, TOK], F32R, outer), sb("x_oa_lo", [P, 4, TOK], F32R, outer))
            ob = Split(sb("x_ob_hi", [P, 4, TOK], F32R, outer), sb("x_ob_lo", [P, 4, TOK], F32R, outer))
            with ExitStack() as scope:
                free = free0
                qz = sb("x_qz", [P, 8, TOK], F32, scope)
                dqz = sb("x_dqz", [P, 8, TOK], F32, scope)
                fkT = sb("x_fkT", [P, 4, TOK], F32, scope)
                ikT = sb("x_ikT", [P, TOK], F32, scope)
                dkT = sb("x_dkT", [P, TOK], F32, scope)
                fv = sb("x_fv", [P, NB, BANK], F32, scope)
                dv = sb("x_dv", [P, NB, 64], F32, scope)
                bias2 = sb("x_bias", [P, D], F32, scope)
                att_p[0] = sb("x_p", [P, 2, D], F32, scope)
                sel = sb("x_sel", [P, NB, TOK], F32, scope)
                iw = sb("x_iw", [P, NB, 8], F32, scope)
                lf = sb("x_lf", [P, NB, 8], F32, scope)
                lt = sb("x_lt", [P, NB, 3, 8], F32, scope)
                cum = sb("x_cum", [P, NB, 8], F32, scope)
                ncumT = sb("x_ncumT", [8, TOK], F32, scope)
                hg = sb("x_hg", [P, 4, 64], F32, scope)
                bf = sb("x_bf", [P, 8], F32, scope)
                top = sb("x_top", [P, NB, 8], F32, scope)
                bias1 = post_g
                nat = work[:, :, 0:BANK]
                small = work[:, :, BANK:D]
                nat_read, small_read = [[None, None] for _ in range(2)]

                def bias_rows(g):
                    return bass.AP(tensor=bias_dram[0].tensor, offset=4 * g * 384, ap=[[1, P], [384, 4], [1, TOK]])

                bias_t = [prog.load("bias_load", t_[:, :].rearrange("p (h s) -> p h s", h=4), bias_rows(g), [*free, *post_read, bias_stored[0]])
                          for g, t_ in ((0, bias1), (1, bias2))]
                small_t = [prog.load("hg_load", hg[:, n, :], d[name].partition_broadcast(P), free)
                           for n, name in enumerate(("fox_q_norm_2", "fox_k_norm_2", "dsa_q_norm_2", "dsa_k_norm_2"))]
                small_t.append(prog.load("hg_load", bf[:, :], d["b_forget_2"].partition_broadcast(P), free))
                zero = [prog.pool("q_zero", lambda e, x=x: e.memset(x, 0.0), free)
                        for t_ in (qz, dqz) for x in (t_[64:128, 0::2, :], t_[0:64, 1::2, :])]

                def spread(b, dst, scale, wait):
                    i, t = transpose([nat[:, b, k * P:(k + 1) * P] for k in range(4)], wait)
                    nat_read[b] = t
                    src = bank(i).rearrange("p (c t) -> p c t", c=4)
                    for q in range(2):
                        rr = slice(64 * q, 64 * q + 64)
                        t = prog.act("q_spread", act(dst[rr, q::2, b * P:(b + 1) * P], src[rr, :, :], ACT.Copy, scale=scale),
                                     [t, *zero, *free])
                    tbank.free[i] = (t,)
                    return t

                def head_norm(b, x, n, done):
                    y = nat[:, b, :].rearrange("p (h c) -> p h c", h=8)
                    x3 = x.rearrange("p (h c) -> p h c", h=8)
                    st = stat[:, b, 48:56]
                    t = prog.act("hn_sq", act(nat[:, b, :], x, ACT.Square, scale=r_(b)), [*done, nat_read[b], r_ready[b], *free])
                    t = prog.dve("hn_sum", lambda e, o=st, i=y: e.reduce_sum(o, i, axis=AX.X), [t, *free])
                    t = prog.dve("hn_ms", ts(st, st, 1.0 / 64, ALU.mult, EPS, ALU.add), [t])
                    prog.pool("hn_rs", tt(st, st, half[:, 0:8], ALU.pow), [t])
                    t = prog.pool("hn_rs", tt(st, st, r_(b).broadcast_to([P, 8]), ALU.mult))
                    yield
                    t = prog.dve("hn_x", tt(y, x3, st.unsqueeze(2).broadcast_to([P, 8, 64]), ALU.mult), [t])
                    bank_free = t
                    t = prog.dve("hn_gain", tt(y, y, hg[:, n, :].unsqueeze(1).broadcast_to([P, 8, 64]), ALU.mult), [t, *small_t])
                    head_out[b] = (bank_free, t)
                    for _ in range(4):
                        yield

                head_out = [None, None]
                iq_ready, ik_ready, lf_ready, dq_ready, fq_ready, fk_ready, fv_ready = [[None, None] for _ in range(7)]
                iw_ready = [None, None]
                index_read = [None, None]

                def first_consumer(b, banks, done):
                    s = bank(banks["S"], 0, 208)
                    t = prog.act("iq_nat", act(nat[:, b, :], bank(banks["I"]), ACT.Copy, scale=r_(b)), [done["I"], nat_read[b], r_ready[b], *free])
                    acc.free[banks["I"]] = (t,)
                    sn = small[:, b, :]
                    prog.dve(None, ts(sn[:, 0:64], s[:, 0:64], r_(b), ALU.mult), [done["S"], small_read[b], r_ready[b], *free])
                    prog.dve(None, ts(sn[:, 64:128], s[:, 0:64], r_(b), ALU.mult))
                    prog.dve(None, ts(sn[:, 128:192], s[:, 72:136], r_(b), ALU.mult))
                    iw_ready[b] = prog.dve("small", ts(iw[:, b, :], s[:, 64:72], r_(b), ALU.mult, 8.0 ** -0.5, ALU.mult))
                    prog.dve(None, ts(dv[:, b, :], s[:, 136:200], r_(b), ALU.mult))
                    z, e1, u1 = lt[:, b, 0, :], lt[:, b, 1, :], lt[:, b, 2, :]
                    tz = prog.dve("small", stt(z, s[:, 200:208], r_(b), ALU.mult, bf[:, :], ALU.add), small_t)
                    acc.free[banks["S"]] = (tz,)
                    rt, token = rms_scale(b, 12, [sn[:, 128:192]], 64, "dk", [tz], junk=sn[:, 256:320])
                    yield
                    tk = prog.dve("dk_norm", ts(sn[:, 128:192], sn[:, 128:192], rt, ALU.mult), [token])
                    tk = prog.dve("dk_gain", tt(sn[:, 128:192], sn[:, 128:192], hg[:, 3, :], ALU.mult), [tk])
                    tk = prog.dve("dk_twice", copy(sn[:, 192:256], sn[:, 128:192]), [tk])
                    iq_ready[b] = spread(b, qz, 1.0, [t])
                    yield
                    i, t = transpose([sn[:, 0:128], sn[:, 128:256]], [tk])
                    small_read[b] = t
                    prog.act(None, act(ikT[:, b * P:(b + 1) * P], bank(i, 0, P), ACT.Copy), [t, *free])
                    ik_ready[b] = prog.act("keysT", act(dkT[:, b * P:(b + 1) * P], bank(i, P, P), ACT.Copy))
                    tbank.free[i] = (ik_ready[b],)
                    t = prog.dve("lf", ts(e1, z, -1.0, ALU.mult), [tz])
                    t = prog.dve("lf", tt(e1, z, e1, ALU.min), [t])
                    t = prog.act("lf_a", act(e1, e1, ACT.Exp), [t])
                    yield
                    t = prog.dve("lf", ts(u1, e1, 1.0, ALU.add), [t])
                    tl = prog.act("lf_a", act(lf[:, b, :], u1, ACT.Ln), [t])
                    t = prog.dve("lf", ts(u1, u1, -1.0, ALU.add, 2.0 ** -24, ALU.max), [tl])
                    t = prog.dve("lf", lambda e, o=u1: e.reciprocal(o, o), [t])
                    yield
                    t = prog.dve("lf", tt(e1, e1, u1, ALU.mult), [t])
                    t = prog.dve("lf", tt(lf[:, b, :], lf[:, b, :], e1, ALU.mult), [t])
                    t = prog.dve("lf", ts(z, z, 0.0, ALU.min), [t])
                    lf_ready[b] = prog.dve("lf", tt(lf[:, b, :], z, lf[:, b, :], ALU.subtract), [t])

                cum_ready = [None, None]

                def cumulate(b):
                    while lf_ready[b] is None:
                        yield
                    while not acc.available():
                        yield
                    i, bfree = acc.take()
                    t = prog.pe("pe_cum", mm(bank(i, 0, 8), upto, lf[:, b, :], True, b == 0), [lf_ready[b], *bfree])
                    if b == 1:
                        t = prog.pe("pe_cum", mm(bank(i, 0, 8), ones, lf[:, 0, :], False, True), [lf_ready[0]])
                    t = prog.dve("cum", copy(cum[:, b, :], bank(i, 0, 8)), [t, *free])
                    acc.free[i] = (t,)
                    yield
                    j, t = transpose([cum[:, b, :]], [t])
                    t = prog.dve("cumT", ts(ncumT[:, b * P:(b + 1) * P], bank(j, 0, P)[0:8, :], -1.0, ALU.mult), [t, *free])
                    tbank.free[j] = (t,)
                    cum_ready[b] = t

                sel_ready = [None, None]

                def index(b):
                    nk, k_top = (b + 1) * P, 64
                    while iq_ready[b] is None or ik_ready[b] is None:
                        yield
                    yield
                    score = sel[:, b, 0:nk]
                    causal = mask[:, P:2 * P] if b == 0 else mask
                    t_s = None
                    for g in range(2):
                        while not acc.available(b + 1):
                            yield
                        i, bfree = acc.take() if b == 0 else acc.take_pair()
                        s = ps_all[:, i * BANK:i * BANK + 4 * nk]
                        for k in range(4):
                            t = prog.pe("pe_index", mm(s[:, k * nk:(k + 1) * nk], qz[:, 4 * g + k, b * P:(b + 1) * P], ikT[:, 0:nk], True, True),
                                        [iq_ready[b], *[x for x in ik_ready if x], *bfree])
                        index_read[b] = t
                        r = att_p[0][:, g, 0:4 * nk]
                        t = prog.act("index_relu", act(r, s, ACT.Relu, scale=64.0 ** -0.5), [t, p_free[g], *free])
                        for u in range(i, i + b + 1):
                            acc.free[u] = (t,)
                        yield
                        for k in range(4):
                            h_ = 4 * g + k
                            t_s = prog.dve("index_sum", stt(score, r[:, k * nk:(k + 1) * nk], iw[:, b, h_:h_ + 1], ALU.mult,
                                                            causal if h_ == 0 else score, ALU.add), [t, t_s, iw_ready[b], *free])
                        p_free[g] = t_s
                        yield
                    t = t_s
                    for n in range(k_top // 8):
                        t = prog.dve("top_max", lambda e, o=top[:, b, :], x=score: e.max(o, x), [t])
                        t = prog.dve("top_take", lambda e, o=score, m=top[:, b, :], x=score: e.match_replace(o, m, x, TAKEN), [t])
                        yield
                    t = prog.dve("sel", ts(score, score, TAKEN / 2, ALU.is_gt, NEG, ALU.mult), [t])
                    sel_ready[b] = prog.dve("sel", tt(score, score, causal, ALU.add), [t])

                background.append((2, index(0)))
                background.append((2, index(1)))
                background.append((2, cumulate(0)))
                background.append((2, cumulate(1)))

                run_group(Group(first_consumer).add(p_iq, [(0, BANK, "I")]).add(p_small, [(0, 208, "S")]), nT)

                def dq_consumer(b, banks, done):
                    yield from head_norm(b, bank(banks["X"]), 2, [done["X"]])
                    acc.free[banks["X"]] = (head_out[b][0],)
                    dq_ready[b] = spread(b, dqz, 0.125, [head_out[b][1]])

                def fk_consumer(b, banks, done):
                    yield from head_norm(b, bank(banks["X"]), 1, [done["X"]])
                    acc.free[banks["X"]] = (head_out[b][0],)
                    i, t = transpose([nat[:, b, k * P:(k + 1) * P] for k in range(4)], [head_out[b][1]])
                    nat_read[b] = t
                    t = prog.act("fkT_out", act(fkT[:, :, b * P:(b + 1) * P], bank(i).rearrange("p (c t) -> p c t", c=4), ACT.Copy), [t, *free])
                    tbank.free[i] = (t,)
                    fk_ready[b] = t

                def fq_consumer(b, banks, done):
                    yield from head_norm(b, bank(banks["X"]), 0, [done["X"]])
                    acc.free[banks["X"]] = (head_out[b][0],)
                    while index_read[0] is None or index_read[1] is None:
                        yield
                    fq_ready[b] = spread(b, qz, 0.125, [head_out[b][1], *index_read])

                def fv_consumer(b, banks, done):
                    t = prog.act("fv_out", act(fv[:, b, :], bank(banks["X"]), ACT.Copy, scale=r_(b)), [done["X"], *free])
                    acc.free[banks["X"]] = (t,)
                    fv_ready[b] = t
                    yield

                for plan_, consumer in ((p_dq, dq_consumer), (p_fk, fk_consumer), (p_fq, fq_consumer), (p_fv, fv_consumer)):
                    run_group(Group(consumer).add(plan_, [(0, BANK, "X")]), nT)
                finish()

                def pair_rows(h_, k):
                    return slice(64 * (h_ % 2), 64 * (h_ % 2) + 64), k // 2

                def fox_scores(b):
                    blk, nk = slice(b * P, (b + 1) * P), (b + 1) * P

                    def queue(h_, out, bfree):
                        prog.pe(None, mm(out, qz[:, h_, blk], fkT[:, h_ // 2, 0:nk], True, False), [*fq_ready, *fk_ready, *bfree])
                        return prog.pe("pe_score", mm(out, ident[0:8, h_:h_ + 1].broadcast_to([8, P]), ncumT[:, 0:nk], False, True), cum_ready)
                    return queue

                def fox_late(b, heads, mx, ng, t):
                    c = cum[:, b, heads[0]:heads[0] + 4]
                    t = prog.dve("fox_max", tt(mx, mx, c, ALU.add), [t])
                    return prog.dve("fox_bias", tt(ng, c, mx, ALU.subtract), [t])

                fox = [attention(b, range(4 * g, 4 * g + 4), n % 2, fox_scores(b),
                                 lambda h_, kb: fv[:, kb, h_ * 64:(h_ + 1) * 64], pair_rows,
                                 acc, put_split(oa, 2 * g, 2, b), [*free, *fv_ready, *nat_read, *small_read],
                                 key_mask=lambda b=b: (mask[:, P:2 * P] if b == 0 else mask, None), late=fox_late)
                       for n, (b, g) in enumerate(((0, 0), (0, 1), (1, 0), (1, 1)))]
                def dsa_scores(b):
                    blk, nk = slice(b * P, (b + 1) * P), (b + 1) * P

                    def queue(h_, out, bfree):
                        prog.pe(None, mm(out, dqz[:, h_, blk], dkT[:, 0:nk], True, False), [*dq_ready, *ik_ready, *bfree])
                        tile = (bias1, bias2)[h_ // 4][:, (h_ % 4) * TOK:(h_ % 4 + 1) * TOK]
                        return prog.pe("pe_score", mm(out, flip, tile[:, TOK - nk:TOK], False, True), bias_t)
                    return queue

                dsa = [attention(b, range(4 * g, 4 * g + 4), n % 2, dsa_scores(b),
                                 lambda h_, kb: dv[:, kb, :], pair_rows,
                                 acc, put_split(ob, 2 * g, 2, b), free,
                                 key_mask=lambda b=b: (sel[:, b, 0:(b + 1) * P], sel_ready[b]))
                       for n, (b, g) in enumerate(((0, 0), (0, 1), (1, 0), (1, 1)))]
                for _ in pipeline(fox + dsa):
                    step_background()
                finish()

            with ExitStack() as scope:
                free = prog.so_far()
                mT = Split(sb("x_m_hi", [P, KT, TOK], F32R, scope), sb("x_m_lo", [P, KT, TOK], F32R, scope))
                gate = sb("x_gate", [P, NB, BANK], F32, scope)
                merged = sb("x_merged", [P, NB, BANK], F32, scope)
                merged_t, merged_read = [None, None], [None, None]

                def half_consumer(first, s):
                    def consumer(b, banks, done):
                        t = prog.act("gate_th", act(gate[:, b, :], bank(banks["G"]), ACT.Tanh, scale=r_half(b)), [done["G"], merged_t[b], *free])
                        acc.free[banks["G"]] = (t,)
                        dst = merged[:, b, :] if first else gate[:, b, :]
                        t = prog.dve("gate_mul", stt(dst, gate[:, b, :], 1.0, ALU.add, bank(banks["O"]), ALU.mult),
                                     [t, done["O"], merged_read[b], *free])
                        acc.free[banks["O"]] = (t,)
                        merged_t[b] = t
                        yield
                        if not first:
                            t = prog.dve("gate_sum", tt(merged[:, b, :], merged[:, b, :], gate[:, b, :], ALU.add), [t])
                            merged_t[b] = t
                            yield
                            i, t = transpose([merged[:, b, k * P:(k + 1) * P] for k in range(4)], [t])
                            merged_read[b] = t
                            yield
                            evacuate_split(i, 4, mT, 4 * s, b, [t], scale=0.5)
                    return consumer

                for s in range(2):
                    ga, wa, gb_, wb = p_merge[s]
                    for first, gate_units, branch_units, o in ((True, ga, wa, oa), (False, gb_, wb, ob)):
                        g = Group(half_consumer(first, s)).add(gate_units, [(0, BANK, "G")], nT).add(branch_units, [(0, BANK, "O")], o)
                        run_group(g, nT)
                g = Group(add_branch(row_next, 1.0, False)).add(p_out, [(0, BANK, "D0"), (BANK, BANK, "D1")])
                run_group(g, mT, lag=7, calm=True)
            outer.close()

        setup = ExitStack()
        rows = sb("rows", [P, P], F32, setup)
        pos_i = sb("pos_i", [P, NB], I32, setup)
        pos = sb("pos", [P, NB], F32, setup)
        invf = sb("invf", [P, 32], F32, setup)
        ang = sb("ang", [P, NB, 2, 32], F32, setup)
        turn = sb("turn", [P, NB, 2, 32], F32, setup)
        onehot = sb("onehot", [32, 384], F32, setup)
        relb = sb("relb", [32, 8], F32, setup)
        biasr = sb("biasr", [8, 384], F32, setup)
        prog.pool("half", lambda e: e.memset(half[:, 0:8], -0.5))
        half_ready[0] = prog.pool("half", lambda e: e.memset(half[:, 8:9], 0.5))
        g_t, x_t = [], []
        for name, r, n in plan:
            a = d[name]
            flat = a.rearrange("a b c -> (a b c)") if len(a.shape) == 3 else a.rearrange("a b -> (a b)") if len(a.shape) == 2 else a
            g_t.append(prog.load("gain_load" if r else "gain0_load", rows[r:r + n, :], flat.rearrange("(r p) -> r p", p=P),
                                 engine="pool" if r else "act"))
            if r == 0:
                c_t = prog.load("cst_load", cst[:, 0:P], d["c_packed"][:, 0:P], engine="act")
                x_t = [prog.load(f"x_load{b}", h[:, b, :], d["x"][0, b * P:(b + 1) * P, :], engine="act" if b else "sp") for b in range(NB)]
                c_rest = prog.load("cst_rest_load", cst[:, P:], d["c_packed"][:, P:], engine="act")
        pos_t = [prog.load("pos_load", pos_i[:, :], d["positions"][0, :].rearrange("(b p) -> p b", p=P),
                           allow_slow_non_contiguous=True),
                 prog.load("pos_load", invf[:, :], d["c_inv_freq"]),
                 prog.load("pos_load", onehot[:, :], d["c_onehot"]),
                 prog.load("pos_load", relb[:, :], d["rel_bias_2"])]

        def gain_table(r0, r1, wait):
            i, free = tbank.take()
            t = prog.pe("pe_tr", tr(bank(i, 0, r1), rows[0:r1, :], ident[0:r1, 0:r1]), [*wait, *free])
            gain_ready[0] = prog.dve("gain_cols", copy(gcol[:, r0:r1], bank(i, r0, r1 - r0)), [t])
            tbank.free[i] = (gain_ready[0],)

        ffns = []
        ffns.append(plan_ffn(d["ffn_w_gate"][0, 0], d["ffn_w_up"][0, 0], d["ffn_w_down"][0, 0]))
        gmlp_in = [plan_cols(d["gmlp_w_in"][0], [(c, c + BANK)]) for c in (*range(2048, 4096, BANK), *range(0, 2048, BANK))]
        gmlp_out = plan_cols(d["gmlp_w_out"][0], [(0, D)])
        ffns.append(plan_ffn(d["ffn_w_gate"][0, 1], d["ffn_w_up"][0, 1], d["ffn_w_down"][0, 1]))
        dkv = plan_cols(d["w_dkv"], [(0, 320)])
        ffns.append(plan_ffn(d["ffn_w_gate"][1, 0], d["ffn_w_up"][1, 0], d["ffn_w_down"][1, 0]))
        ukv = [plan_cols(d["w_ukv"], [(c, c + D)]) for c in (0, D)]
        dq_lat = plan_cols(d["mla_w_dq"][0], [(0, BANK)])
        uq = [plan_cols(d["mla_w_uq"][0], [(c, c + 768)]) for c in (0, 768)]
        w_o = plan_cols(d["mla_w_o"][0], [(0, D)])
        ffns.append(plan_ffn(d["ffn_w_gate"][1, 1], d["ffn_w_up"][1, 1], d["ffn_w_down"][1, 1]))
        ffns.append(plan_ffn(d["ffn1_w_gate_2"], d["ffn1_w_up_2"], d["ffn1_w_down_2"]))
        FQ, FK, FV, FF, DQ, DK, IQ, IK, GA, GB = 0, 512, 1024, 1536, 1544, 2056, 2184, 2696, 2768, 3792
        w_in = d["w_in_2"]
        p_iq = plan_cols(w_in, [(IQ, IQ + 512)])
        p_small = plan_cols(w_in, [(IK, IK + 72), (DK, DK + 128), (FF, FF + 8)])
        p_dq = plan_cols(w_in, [(DQ, DQ + 512)])
        p_fk = plan_cols(w_in, [(FK, FK + 512)])
        p_fq = plan_cols(w_in, [(FQ, FQ + 512)])
        p_fv = plan_cols(w_in, [(FV, FV + 512)])
        p_merge = []
        for c in (0, BANK):
            p_merge.append([plan_cols(w_in, [(GA + c, GA + c + BANK)]),
                            plan_cols(d["w_branch_a_2"], [(c, c + BANK)]),
                            plan_cols(w_in, [(GB + c, GB + c + BANK)]),
                            plan_cols(d["w_branch_b_2"], [(c, c + BANK)])])
        p_out = plan_cols(d["w_out_2"], [(0, D)])
        ffns.append(plan_ffn(d["ffn2_w_gate_2"], d["ffn2_w_up_2"], d["ffn2_w_down_2"]))
        W.pump(3)
        n_first = plan[0][2]
        gain_table(0, n_first, [c_t, g_t[0]])
        for _ in h_to_nT(0, row_of["ffn_pre_g"], [x_t[0]] * 2):
            pass
        measure(0, [x_t[0]])

        def second_block():
            yield from h_to_nT(1, row_of["ffn_pre_g"], [x_t[1]] * 2)
            measure(1, [x_t[1]])

        background.append((1, second_block()))

        def tables():
            yield
            gain_table(n_first, n_rows, [c_rest, *g_t])
            yield

            t = prog.dve("pos_f", copy(pos[:, :], pos_i[:, :]), pos_t)
            for b in range(NB):
                for q, shift in ((0, 0.25), (1, 0.0)):
                    yield
                    a, r = ang[:, b, q, :], turn[:, b, q, :]
                    t = prog.dve("rope", ts(a, invf[:, :], pos[:, b:b + 1], ALU.mult), [t])
                    t = prog.dve("rope", ts(r, a, 1.0 / (2 * math.pi), ALU.mult, shift, ALU.add), [t])
                    t = prog.dve("rope", ts(r, r, 12582912.0, ALU.add, -12582912.0, ALU.add), [t])
                    rest = 2 * math.pi
                    for bits in (8, 11, 24):
                        scale = 2.0 ** (bits - 1 - math.floor(math.log2(rest)))
                        part = math.floor(rest * scale) / scale if bits < 24 else rest
                        rest -= part
                        t = prog.dve("rope", stt(a, r, -part, ALU.mult, a, ALU.add), [t])
                    if q == 0:
                        t = prog.dve("rope", ts(a, a, math.pi / 2, ALU.add), [t])
                    t = prog.dve("rope", ts(a, a, 3.1415925, ALU.min, -3.1415925, ALU.max), [t])
            rope_ready[0] = prog.act("rope_sin", act(rope[:, :, :, :], ang[:, :, :, :], ACT.Sin), [t])

            i, free = tbank.take()
            t = prog.pe("pe_bias", mm(bank(i, 0, 384)[0:8, :], relb[:, :], onehot[:, :], True, True), [*pos_t, *free])
            t = prog.dve("bias_rows", copy(biasr[:, :], bank(i, 0, 384)[0:8, :]), [t])
            tbank.free[i] = (t,)
            bias_stored[0] = prog.load("bias_store", bias_dram, biasr[:, :], [t])

        background.append((2, tables()))

        R = row_of
        latents = ExitStack()
        state = {}

        def stage_kv():
            cT = Split(sb("cT_hi", [P, 2, TOK], F32R, latents), sb("cT_lo", [P, 2, TOK], F32R, latents))
            krT = sb("krT", [P, TOK], F32, latents)
            state["kv"] = (cT, krT)
            shared_kv_down(R["ffn_pre_g"] + 16, cT, krT, latents)

        def stage_mla():
            mla(R["ffn_pre_g"] + 24, *state["kv"])
            latents.close()

        def stage_first():
            ffn("f0", ffns[0], R["mix_pre_g"], 0.5, d["ffn_post_g"][0, 0])
            setup.close()

        stages = [
            stage_first,
            lambda: gmlp(R["ffn_pre_g"] + 8),
            lambda: ffn("f1", ffns[1], R["kv_norm_g"], 0.5, d["ffn_post_g"][0, 1]),
            lambda: (stage_kv(), ffn("f2", ffns[2], R["mix_pre_g"] + 8, 0.5, d["ffn_post_g"][1, 0])),
            stage_mla,
            lambda: ffn("f3", ffns[3], R["ffn1_norm_2"], 0.5, d["ffn_post_g"][1, 1]),
            lambda: ffn("f4", ffns[4], R["mix_norm_2"], 0.5, None),
            lambda: mixer2(R["ffn2_norm_2"]),
            lambda: ffn("f5", ffns[5], None, 0.5, None),
        ]
        for stage in stages[:stop_after]:
            stage()
        finish()
        latents.close()
        outs = [prog.load(f"out_store{b}", out[0, b * P:(b + 1) * P, :], h[:, b, :], [h_ready[b]], engine="sp") for b in range(NB)]
        prog.op("sp", None, lambda e: None, outs)

        with nc.Block() as block:
            block.sync(lambda e: prog.play("sp", e))
            block.gpsimd(lambda e: prog.play("pool", e))
            block.scalar(lambda e: prog.play("act", e))
            block.tensor(lambda e: prog.play("pe", e))
            block.vector(lambda e: prog.play("dve", e))


def kernel(**inputs):
    import concourse.bacc as bacc
    from concourse.bass_utils import run_bass_kernel_spmd

    nc = bacc.Bacc("TRN2", target_bir_lowering=False, num_devices=1)
    arrays, d = {}, {}
    for name, a in {**inputs, **constants()}.items():
        a = np.ascontiguousarray(a)
        arrays[f"in_{name}"] = a
        d[name] = nc.dram_tensor(f"in_{name}", a.shape, mybir.dt.from_np(a.dtype), kind="ExternalInput").ap()
    out = nc.dram_tensor("out_0", (1, TOK, D), F32, kind="ExternalOutput").ap()
    build(nc, d, out)
    return run_bass_kernel_spmd(nc, [arrays], core_ids=[0]).results[0]["out_0"]
```
